# Optimizing a Trainium2 kernel written in Bass

```python
import math
import jax, jax.numpy as jnp
from jax import lax
import numpy as np

D_MODEL = 1024
BATCH = 1
SEQ = 1024
DEPTH = 2
DEC_BATCH = 8
DEC_SEQ = 4
PAST_LEN = 256
PAGE_SIZE = 128

N_A_LAYERS = DEPTH // 2
N_B_LAYERS = DEPTH - N_A_LAYERS
POOL_WINDOWS = (2, 4, 8, 16)
N_POOL_GROUPS = len(POOL_WINDOWS)
POOL_GROUP_DIM = D_MODEL // N_POOL_GROUPS
POOL_BUF = max(POOL_WINDOWS) - 1
N_HEADS = 16
HEAD_DIM = D_MODEL // N_HEADS
D_FF = 4 * D_MODEL
Q_BLOCK = 128
EPS = 1e-6
FORGET_BIAS = 4.0

kernel_name = "yoco_pool_fox_decoder_step"

def rmsnorm(x, g):
    xf = x.astype(jnp.float32)
    y = xf * lax.rsqrt(jnp.mean(xf * xf, axis=-1, keepdims=True) + EPS)
    return (y * g.astype(jnp.float32)).astype(x.dtype)

def sq_relu_mlp(h, g, w_up, w_down):
    a = jax.nn.relu(rmsnorm(h, g) @ w_up)
    return (a * a) @ w_down

def pool_mixer(xn_ext, pos, w_grp, scale):
    B = xn_ext.shape[0]
    T = pos.shape[0]
    xf = xn_ext.astype(jnp.float32)
    cs = jnp.concatenate([jnp.zeros_like(xf[:, :1]), jnp.cumsum(xf, axis=1)], axis=1)
    end = cs[:, POOL_BUF + 1:]
    x_new = xf[:, POOL_BUF:]
    outs = []
    for gi, w in enumerate(POOL_WINDOWS):
        sl = slice(gi * POOL_GROUP_DIM, (gi + 1) * POOL_GROUP_DIM)
        start = cs[:, POOL_BUF + 1 - w: POOL_BUF + 1 - w + T, sl]
        cnt = jnp.minimum(pos + 1, w).astype(jnp.float32)[None, :, None]
        outs.append((end[..., sl] - start) / cnt - x_new[..., sl])
    pooled = jnp.stack(outs, axis=2)
    mixed = jnp.einsum('btgc,gcd->btgd', pooled, w_grp.astype(jnp.float32)).reshape(B, T, D_MODEL)
    return (mixed * scale.astype(jnp.float32)).astype(xn_ext.dtype)

def a_layers(h, pool_prefix, pos, g_pool, w_pool, pool_scale, g_mlp, w_up, w_down):
    bufs = []
    for l in range(N_A_LAYERS):
        xn = rmsnorm(h, g_pool[l])
        ext = jnp.concatenate([pool_prefix[l].astype(xn.dtype), xn], axis=1)
        h = h + pool_mixer(ext, pos, w_pool[l], pool_scale[l])
        h = h + sq_relu_mlp(h, g_mlp[l], w_up[l], w_down[l])
        bufs.append(ext[:, -POOL_BUF:])
    return h, jnp.stack(bufs, axis=0)

def shared_kv(h, g_kv, w_k, w_v, g_k, w_f, b_f):
    B, T, _ = h.shape
    hn = rmsnorm(h, g_kv)
    k = rmsnorm((hn @ w_k).reshape(B, T, N_HEADS, HEAD_DIM), g_k)
    v = (hn @ w_v).reshape(B, T, N_HEADS, HEAD_DIM)
    logf = jax.nn.log_sigmoid((hn @ w_f).astype(jnp.float32) + b_f.astype(jnp.float32))
    return k, v, logf

def fox_attend(q, k, v, cq, ck, q_pos, k_pos):
    s = jnp.einsum('bqhd,bkhd->bhqk', q, k, preferred_element_type=jnp.float32) * (1.0 / math.sqrt(HEAD_DIM))
    decay = jnp.transpose(cq, (0, 2, 1))[..., :, None] - jnp.transpose(ck, (0, 2, 1))[..., None, :]
    mask = k_pos[None, :] <= q_pos[:, None]
    s = jnp.where(mask[None, None], s + decay, -jnp.inf)
    p = jax.nn.softmax(s, axis=-1)
    return jnp.einsum('bhqk,bkhd->bqhd', p.astype(v.dtype), v)

def fox_prompt(q, k, v, c):
    B, T, H, hd = q.shape
    nb = T // Q_BLOCK
    qb = q.reshape(B, nb, Q_BLOCK, H, hd).transpose(1, 0, 2, 3, 4)
    cb = c.reshape(B, nb, Q_BLOCK, H).transpose(1, 0, 2, 3)
    pb = jnp.arange(T, dtype=jnp.int32).reshape(nb, Q_BLOCK)
    kpos = jnp.arange(T, dtype=jnp.int32)
    out = lax.map(lambda a: fox_attend(a[0], k, v, a[1], c, a[2], kpos), (qb, cb, pb))
    return out.transpose(1, 0, 2, 3, 4).reshape(B, T, H, hd)

def b_layers(h, attend, g_attn, w_q, g_q, w_o, g_mlp, w_up, w_down):
    B, T, _ = h.shape
    for l in range(N_B_LAYERS):
        q = rmsnorm((rmsnorm(h, g_attn[l]) @ w_q[l]).reshape(B, T, N_HEADS, HEAD_DIM), g_q[l])
        o = attend(q).reshape(B, T, D_MODEL)
        h = h + o @ w_o[l]
        j = N_A_LAYERS + l
        h = h + sq_relu_mlp(h, g_mlp[j], w_up[j], w_down[j])
    return h

def setup_inputs(seed: int = 0) -> dict:
    key = jax.random.key(seed)
    ks = jax.random.split(key, 32)
    n_pages = PAST_LEN // PAGE_SIZE
    n_used = DEC_BATCH * n_pages
    n_pool = n_used + n_used // 4
    nrm = lambda k, shp, s: jax.random.normal(k, shp, jnp.float32) * s
    x_prompt = nrm(ks[0], (BATCH, SEQ, D_MODEL), 1.0)
    x_sample = nrm(ks[1], (DEC_BATCH, DEC_SEQ, D_MODEL), 1.0)
    state_pool = nrm(ks[2], (N_A_LAYERS, DEC_BATCH, POOL_BUF, D_MODEL), 1.0)
    cache_k = nrm(ks[3], (n_pool, PAGE_SIZE, N_HEADS, HEAD_DIM), 1.0)
    cache_v = nrm(ks[4], (n_pool, PAGE_SIZE, N_HEADS, HEAD_DIM), 1.0)
    cache_logf = jax.nn.log_sigmoid(FORGET_BIAS + nrm(ks[5], (n_pool, PAGE_SIZE, N_HEADS), 1.0))
    page_table = jax.random.permutation(ks[6], n_pool)[:n_used].reshape(DEC_BATCH, n_pages).astype(jnp.int32)
    g_pool = 1.0 + nrm(ks[7], (N_A_LAYERS, D_MODEL), 0.05)
    w_pool = nrm(ks[8], (N_A_LAYERS, N_POOL_GROUPS, POOL_GROUP_DIM, POOL_GROUP_DIM), POOL_GROUP_DIM ** -0.5)
    pool_scale = 1.0 + nrm(ks[9], (N_A_LAYERS, D_MODEL), 0.1)
    g_attn = 1.0 + nrm(ks[10], (N_B_LAYERS, D_MODEL), 0.05)
    w_q = nrm(ks[11], (N_B_LAYERS, D_MODEL, D_MODEL), D_MODEL ** -0.5)
    g_q = 1.0 + nrm(ks[12], (N_B_LAYERS, HEAD_DIM), 0.05)
    w_o = nrm(ks[13], (N_B_LAYERS, D_MODEL, D_MODEL), D_MODEL ** -0.5)
    g_kv = 1.0 + nrm(ks[14], (D_MODEL,), 0.05)
    w_k = nrm(ks[15], (D_MODEL, D_MODEL), D_MODEL ** -0.5)
    w_v = nrm(ks[16], (D_MODEL, D_MODEL), D_MODEL ** -0.5)
    g_k = 1.0 + nrm(ks[17], (HEAD_DIM,), 0.05)
    w_f = nrm(ks[18], (D_MODEL, N_HEADS), D_MODEL ** -0.5)
    b_f = FORGET_BIAS + nrm(ks[19], (N_HEADS,), 0.1)
    g_mlp = 1.0 + nrm(ks[20], (DEPTH, D_MODEL), 0.05)
    w_up = nrm(ks[21], (DEPTH, D_MODEL, D_FF), D_MODEL ** -0.5)
    w_down = nrm(ks[22], (DEPTH, D_FF, D_MODEL), D_FF ** -0.5)
    return {"x_prompt": x_prompt, "x_sample": x_sample, "state_pool": state_pool,
            "cache_k": cache_k, "cache_v": cache_v, "cache_logf": cache_logf, "page_table": page_table,
            "g_pool": g_pool, "w_pool": w_pool, "pool_scale": pool_scale,
            "g_attn": g_attn, "w_q": w_q, "g_q": g_q, "w_o": w_o,
            "g_kv": g_kv, "w_k": w_k, "w_v": w_v, "g_k": g_k, "w_f": w_f, "b_f": b_f,
            "g_mlp": g_mlp, "w_up": w_up, "w_down": w_down}

def reference(x_prompt, x_sample, state_pool, cache_k, cache_v, cache_logf, page_table,
              g_pool, w_pool, pool_scale, g_attn, w_q, g_q, w_o,
              g_kv, w_k, w_v, g_k, w_f, b_f, g_mlp, w_up, w_down):
    Bp, Tp, _ = x_prompt.shape
    pos_p = jnp.arange(Tp, dtype=jnp.int32)
    zero_prefix = jnp.zeros((N_A_LAYERS, Bp, POOL_BUF, D_MODEL), x_prompt.dtype)
    h_p, pool_state_prompt = a_layers(x_prompt, zero_prefix, pos_p, g_pool, w_pool, pool_scale, g_mlp, w_up, w_down)
    k_p, v_p, logf_p = shared_kv(h_p, g_kv, w_k, w_v, g_k, w_f, b_f)
    c_p = jnp.cumsum(logf_p, axis=1)
    y_prompt = b_layers(h_p, lambda q: fox_prompt(q, k_p, v_p, c_p),
                        g_attn, w_q, g_q, w_o, g_mlp, w_up, w_down)

    Bs, Ts, _ = x_sample.shape
    past = page_table.shape[1] * PAGE_SIZE
    pos_s = past + jnp.arange(Ts, dtype=jnp.int32)
    h_s, pool_state_sample = a_layers(x_sample, state_pool, pos_s, g_pool, w_pool, pool_scale, g_mlp, w_up, w_down)
    k_s, v_s, logf_s = shared_kv(h_s, g_kv, w_k, w_v, g_k, w_f, b_f)
    k_past = cache_k[page_table].reshape(Bs, past, N_HEADS, HEAD_DIM)
    v_past = cache_v[page_table].reshape(Bs, past, N_HEADS, HEAD_DIM)
    logf_past = cache_logf[page_table].reshape(Bs, past, N_HEADS).astype(jnp.float32)
    k_all = jnp.concatenate([k_past.astype(k_s.dtype), k_s], axis=1)
    v_all = jnp.concatenate([v_past.astype(v_s.dtype), v_s], axis=1)
    c_all = jnp.cumsum(jnp.concatenate([logf_past, logf_s], axis=1), axis=1)
    c_new = c_all[:, past:]
    k_pos = jnp.arange(past + Ts, dtype=jnp.int32)
    y_sample = b_layers(h_s, lambda q: fox_attend(q, k_all, v_all, c_new, c_all, pos_s, k_pos),
                        g_attn, w_q, g_q, w_o, g_mlp, w_up, w_down)

    logf_prompt = logf_p.astype(cache_logf.dtype)
    logf_sample = logf_s.astype(cache_logf.dtype)
    return (y_prompt, y_sample, pool_state_prompt, pool_state_sample,
            k_p, v_p, logf_prompt, k_s, v_s, logf_sample)


_drawn_inputs = setup_inputs


def setup_inputs(seed=0):
    import zlib

    import numpy as np

    out = dict(_drawn_inputs(seed))
    spreads = {}
    factors = {'cache_logf': 4.587, 'g_attn': 8.0, 'g_q': 8.0}
    for name, (base, spread) in spreads.items():
        noise = np.random.default_rng([zlib.crc32(name.encode()), seed]).standard_normal(out[name].shape)
        drawn = base * np.exp(spread * noise) if base else spread * noise
        out[name] = __import__('jax').numpy.asarray(drawn.astype(out[name].dtype))
    for name, factor in factors.items():
        out[name] = (out[name] * factor).astype(out[name].dtype)
    return out
```

```python
from contextlib import ExitStack

import concourse.bass as bass
from concourse import mybir

F32 = mybir.dt.float32
F32R = mybir.dt.float32r
BF16 = mybir.dt.bfloat16
I32 = mybir.dt.int32
ALU = mybir.AluOpType
ACT = mybir.ActivationFunctionType
AX = mybir.AxisListType.X

P = 128
BIG = 1.0e30


def decoder_step(nc, ins, outs):
    x_prompt, x_sample, state_pool = ins["x_prompt"], ins["x_sample"], ins["state_pool"]
    cache_k, cache_v, cache_logf = ins["cache_k"], ins["cache_v"], ins["cache_logf"]
    page_table = ins["page_table"]
    w_up, w_down = ins["w_up"], ins["w_down"]
    y_p, y_s, st_p, st_s, k_p, v_p, lf_p, k_s, v_s, lf_s = outs

    _, T, D = x_prompt.shape
    NB, TS, _ = x_sample.shape
    BUF = state_pool.shape[2]
    NPOOL, PAGE, NH, HD = cache_k.shape
    F = w_up.shape[2]
    S = NB * TS
    N = T + S
    KT = D // P
    NC = 3
    CH = N // NC
    GT = 4
    NG = F // (GT * P)
    NQ = T // P
    NTT = NQ + 1
    EXT = BUF + TS
    NE = BUF + T + NB * EXT
    NKEY = 2 * PAGE + S
    R = NH * TS
    EPS = 1e-6
    WINDOWS = (2, 4, 8, 16)
    assert PAGE == P and T % 512 == 0 and N % NC == 0 and S == 32 and HD == 64 and NG % 2 == 0

    def chunk(c):
        return slice(c * CH, (c + 1) * CH)

    with ExitStack() as ctx:
        base = (nc.sbuf_base + 31) // 32 * 32
        place = {"at": base}

        def region(nbytes):
            at = place["at"]
            place["at"] = at + (nbytes + 31) // 32 * 32
            return at

        def at(name, shape, dt, offset):
            return nc.alloc_sbuf_tensor_at(name, shape, dt, offset=(offset + 31) // 32 * 32)

        def sb(name, shape, dt):
            size = 4 if dt != BF16 else 2
            for s in shape[1:]:
                size *= s
            return at(name, shape, dt, region(size))

        def sem(name):
            return ctx.enter_context(nc.semaphore(name))

        h = sb("h", [P, KT, N], F32)
        xn_at = region(2 * KT * N * 4)
        xn_hi = at("xn_hi", [P, KT, N], F32R, xn_at)
        xn_lo = at("xn_lo", [P, KT, N], F32R, xn_at + KT * N * 4)
        d_at = region(2 * KT * N * 4)
        d2_at = d_at + KT * N * 4
        hid_hi = at("hid_hi", [P, 2 * GT, N], F32R, d_at)
        hid_lo = at("hid_lo", [P, 2 * GT, N], F32R, d2_at)
        norm_tmp = at("norm_tmp", [P, NC, KT, CH], F32, d2_at)
        qT = at("qT", [P, KT, N], F32, d_at)
        kT = at("kT", [P, KT, N], F32, d2_at)
        w_raw = sb("w_raw", [P, 2, KT * P], F32)
        w_hi = sb("w_hi", [P, 2, KT * P], F32R)
        w_lo = sb("w_lo", [P, 2, KT * P], F32R)
        tmp_a_at = place["at"]
        tmp_a = sb("tmp_a", [P, NC, CH], F32)
        tmp_b = sb("tmp_b", [P, NC, CH], F32)
        rms = sb("rms", [P, NC, CH], F32)
        ident = sb("ident", [P, P], F32)
        ones = sb("ones", [P, P], F32)
        vecs = sb("vecs", [P, 6 * KT], F32)
        gains = sb("gains", [P, 3], F32)
        eps_c = sb("eps_c", [P, 1], F32)
        bias_f = sb("bias_f", [NH, 1], F32)
        lfT = sb("lfT", [P, NTT, NH], F32)
        small = sb("small", [P, 16], F32)
        pt_sb = sb("pt_sb", [1, 2 * NB], I32)
        assert place["at"] <= nc.sbuf_usable_end, (place["at"], nc.sbuf_usable_end)

        ext = at("ext", [P, KT, NE], F32, d_at)
        win = [at(f"win{i}", [P, 2, NE], F32, d_at + KT * NE * 4 + i * 2 * NE * 4) for i in range(2)]
        x_tok = at("x_tok", [P, 2, D], F32, xn_at)
        vec_rows = at("vec_rows", [6 * KT, P], F32, xn_at + 2 * D * 4)
        pre_tok = at("pre_tok", [NB * BUF, D], F32, xn_at + 3 * D * 4)
        cnt_i = sb("cnt_i", [P, 16], I32)
        cnt_r = sb("cnt_r", [P, 16], F32)
        pool_tmp = at("pool_tmp", [P, NC, KT, CH], F32, xn_at + 6 * D * 4)

        block_ones = at("block_ones", [P, P], F32, region(P * 4))
        o_tok_at = region(NTT * P * 4)
        o_tok = at("o_tok", [P, NTT, P], F32, o_tok_at)
        st_tok = at("st_tok", [BUF + S, D], F32, o_tok_at)
        st_cols = at("st_cols", [P, KT, BUF + S], F32, tmp_a_at)
        y_tok = at("y_tok", [P, 2, D], F32, xn_at)
        lf_z, lf_a, lf_e, lf_u, lf_l = (at(f"lf_{n}", [NH, N], F32, d2_at + i * N * 4) for i, n in enumerate("zaeul"))
        wf_sb = at("wf_sb", [P, KT, NH], F32, region(KT * NH * 4))
        assert place["at"] <= nc.sbuf_usable_end, (place["at"], nc.sbuf_usable_end)

        a = xn_at
        def att(name, shape, dt=F32):
            nonlocal a
            size = 4 if dt != BF16 else 2
            for s in shape[1:]:
                size *= s
            t = at(name, shape, dt, a)
            a += (size + 31) // 32 * 32
            return t
        k_pg = att("k_pg", [P, 2, D])
        v_pg = att("v_pg", [P, 2, D])
        lf_pg = att("lf_pg", [P, 2, NH])
        lf_pb = att("lf_pb", [P, 2, NH, TS])
        kTa = att("kTa", [P, KT, NKEY])
        q_bd = att("q_bd", [P, KT * 72], F32)
        v_new = att("v_new", [S, D])
        after = att("after", [P, 3, NKEY])
        own = att("own", [S, NB, NH, TS])
        own_neg = att("own_neg", [S, NB, NH, TS])
        lf_new = att("lf_new", [S, NH, TS])
        neg_b = att("neg_b", [S, NH, TS])
        p_s = att("p_s", [R, NKEY])
        pT_s = att("pT_s", [P, 3, R])
        assert a <= xn_at + 2 * KT * N * 4
        a = xn_at
        q_aug = [att(f"q_aug{i}", [P, T]) for i in range(2)]
        k_aug = [att(f"k_aug{i}", [P, T]) for i in range(2)]
        v_h = [att(f"v_h{i}", [P, NQ, HD]) for i in range(2)]
        probs = [att(f"probs{i}", [P, T]) for i in range(2)]
        probsT = att("probsT", [P, NQ, 512])
        ident_b = att("ident_b", [P, P], BF16)
        causal_b = att("causal_b", [P, P], BF16)
        stat = att("stat", [P, 4, 2])
        cum = att("cum", [NH, T])
        ncum = att("ncum", [NH, T])
        zero_r = att("zero_r", [NH, T])
        assert a <= xn_at + 2 * KT * N * 4
        lf_row = rms[0:NH, :, :].rearrange("p c t -> p (c t)")

        ps = ctx.enter_context(nc.psum_tensor("ps", [P, 8, 512], F32))
        cum_dram = nc.dram_tensor("cum_dram", [2, NH, T], F32, kind="Internal").ap()

        w_in = [sem(f"w_in{i}") for i in range(2)]
        w_split, w_used = sem("w_split"), sem("w_used")
        out_dma = sem("out_dma")
        const_ready, passed = sem("const_ready"), sem("passed")

        n_pool, n_mlp = 2, 2 * NG * GT
        n_of = {"pool": 0, "mlp0": n_pool, "q": n_pool + n_mlp}
        n_of["k"] = n_of["q"] + KT
        n_of["v"] = n_of["k"] + KT
        n_of["o"] = n_of["v"] + KT
        n_of["mlp1"] = n_of["o"] + KT
        pool_view = ins["w_pool"].rearrange("l (b g) (c p) d -> (l b) g p c d", b=2, p=P)

        def wait_past(eng, semaphore, value):
            if not isinstance(value, int) or value > 0:
                eng.wait_ge(semaphore, value)

        def apart(eng):
            eng.sem_inc(passed, 1)

        def weights_in(sp):
            def load(n, par, src, k, dst=None):
                if not isinstance(n, int) or n >= 2:
                    sp.wait_ge(w_split, n * 2 - 2)
                d = w_raw[:, par, :].rearrange("p (k c) -> p k c", k=k) if dst is None else dst
                sp.dma_start(d, src).then_inc(w_in[par], 16)
            for b in range(2):
                sp_wait = b
                for g in range(2):
                    d = w_raw[:, b, g * 512:(g + 1) * 512].rearrange("p (k c) -> p k c", k=2)
                    sp.dma_start(d, pool_view[b, g]).then_inc(w_in[b], 8 * 2)
            def up(l, n, par, u):
                v = w_up[l].rearrange("(k p) (u c) -> u p k c", p=P, c=P)
                load(n, par, v[bass.ds(u, 1)].rearrange("o p k c -> (o p) k c"), KT)
            def down(l, n, par, g, q):
                v = w_down[l].rearrange("(g k p) (q c) -> q g p k c", k=GT, p=P, c=2 * P)[q]
                load(n, par, v[bass.ds(g, 1)].rearrange("o p k c -> (o p) k c"), GT)
            def mlp(l):
                b0 = n_of[f"mlp{l}"]
                for j in range(GT):
                    up(l, b0 + j, j % 2, j)
                def group(g, n):
                    for j in range(GT):
                        up(l, n + j, j % 2, g * GT + (GT + j))
                    for q in range(GT):
                        down(l, n + (GT + q), q % 2, g, q)
                with sp.Fori(0, NG - 1, 1) as g:
                    group(g, g * (2 * GT) + (b0 + GT))
                for q in range(GT):
                    down(l, b0 + 2 * GT * NG - GT + q, q % 2, NG - 1, q)
            def square(name, w):
                v = w.rearrange("(k p) (u c) -> u p k c", p=P, c=P)
                with sp.Fori(0, KT // 2, 1) as i:
                    for j in range(2):
                        load(i * 2 + (n_of[name] + j), j, v[bass.ds(i * 2 + j, 1)].rearrange("o p k c -> (o p) k c"), KT)
            mlp(0)
            square("q", ins["w_q"][0])
            square("k", ins["w_k"])
            square("v", ins["w_v"])
            sample_sp(sp)
            prompt_sp(sp)
            square("o", ins["w_o"][0])
            mlp(1)

        n_blocks = n_of["mlp1"] + n_mlp

        def split_weights(pool, n0, count):
            def one(n, par, k16, first):
                pool.wait_ge(w_in[par], k16)
                if not first:
                    pool.wait_ge(w_used, n - 1)
                    apart(pool)
                pool.tensor_copy(w_hi[:, par, :], w_raw[:, par, :]).then_inc(w_split, 1)
                pool.wait_ge(w_split, n * 2 + 1)
                pool.tensor_tensor(w_lo[:, par, :], w_raw[:, par, :], w_hi[:, par, :].bitcast(F32),
                                   ALU.subtract).then_inc(w_split, 1)
            if n0 == 0:
                for n in range(2):
                    one(n, n, 32, True)
                n0, count = 2, count - 2
            if count:
                with pool.Fori(0, count // 2, 1) as i:
                    for j in range(2):
                        one(i * 2 + (n0 + j), j, i * 16 + (16 * (n0 // 2) + 32), False)

        def products(pe, par, cols, nk, c, bank, x_hi, x_lo, stride=P, off=0, frees=False):
            for k in range(nk):
                at_ = off + k * stride
                wh, wl = w_hi[:, par, at_:at_ + P], w_lo[:, par, at_:at_ + P]
                for i, (w, x) in enumerate(((wl, x_hi), (wh, x_lo), (wh, x_hi))):
                    last = pe.matmul(ps[:, bank, 0:CH], w, x(k, c), start=(k == 0 and i == 0),
                                     stop=(k == nk - 1 and i == 2))
                    if frees and k == 0 and i == 0:
                        last.then_inc(w_used, 1)
            return last

        def xh(k, c):
            return xn_hi[:, k, chunk(c)]

        def xl(k, c):
            return xn_lo[:, k, chunk(c)]

        class Norm:
            def __init__(self, name, gain, stats=True, tmp=norm_tmp, plain=False, ready=None, free=None):
                self.ready, self.free = ready, free
                self.name, self.gain, self.stats, self.tmp, self.plain = name, gain, stats, tmp, plain
                (self.sq, self.red, self.sum, self.root, self.rec, self.xn, self.hi, self.lo) = (
                    sem(f"{name}_{s}") if s not in (("xn", "hi", "lo") if plain else () if stats else
                                                    ("sq", "red", "sum", "root", "rec")) else None
                    for s in ("sq", "red", "sum", "root", "rec", "xn", "hi", "lo"))

            def act(self, act):
                def square(c):
                    act.activation(self.tmp[:, c], h[:, :, chunk(c)], ACT.Square).then_inc(self.sq, 1)
                def root(c):
                    act.wait_ge(self.sum, c + 1)
                    act.activation(rms[:, c], ps[:, c, 0:CH], ACT.Sqrt, bias=eps_c[:, 0:1],
                                   scale=1.0 / D).then_inc(self.root, 1)
                def hi(c):
                    act.wait_ge(self.xn, KT * (c + 1))
                    if self.free and c == 0:
                        act.wait_ge(*self.free)
                    act.activation(xn_hi[:, :, chunk(c)], self.tmp[:, c], ACT.Copy).then_inc(self.hi, 1)
                if self.ready:
                    act.wait_ge(*self.ready)
                if self.stats:
                    square(0)
                    square(1)
                    root(0)
                    square(2)
                    root(1)
                    if not self.plain:
                        hi(0)
                    root(2)
                    if not self.plain:
                        hi(1)
                        hi(2)
                else:
                    for c in range(NC):
                        hi(c)

            def pe(self, pe):
                if not self.stats:
                    return
                for c in range(NC):
                    pe.wait_ge(self.red, c + 1)
                    pe.matmul(ps[:, c, 0:CH], ones[:, :], tmp_b[:, c, :], start=True,
                              stop=True).then_inc(self.sum, 1)

            def dve(self, dve, write=None):
                def reduce(c):
                    dve.wait_ge(self.sq, c + 1)
                    dve.tensor_reduce(tmp_b[:, c, :], self.tmp[:, c].rearrange("p k t -> p t k"), AX,
                                      ALU.add).then_inc(self.red, 1)
                def scale(c):
                    if self.stats:
                        dve.wait_ge(self.root, c + 1)
                        dve.reciprocal(rms[:, c], rms[:, c]).then_inc(self.rec, 1)
                        dve.wait_ge(self.rec, c + 1)
                    if write:
                        write(c)
                        return
                    for k in range(KT):
                        dve.scalar_tensor_tensor(self.tmp[:, c, k, :], h[:, k, chunk(c)],
                                                 vecs[:, self.gain * KT + k:self.gain * KT + k + 1],
                                                 rms[:, c], ALU.mult, ALU.mult).then_inc(self.xn, 1)
                if self.ready:
                    dve.wait_ge(*self.ready)
                if self.stats:
                    reduce(0)
                    reduce(1)
                    scale(0)
                    reduce(2)
                    scale(1)
                    scale(2)
                else:
                    for c in range(NC):
                        scale(c)

            def pool(self, pool):
                for c in range(NC):
                    pool.wait_ge(self.hi, c + 1)
                    pool.tensor_tensor(xn_lo[:, :, chunk(c)], self.tmp[:, c], xn_hi[:, :, chunk(c)].bitcast(F32),
                                       ALU.subtract).then_inc(self.lo, 1)

        mixed = sem("mixed")
        m_added = [sem("m0_added"), sem("m1_added")]
        o_added = sem("o_added")
        norm_pool = Norm("np", 0, tmp=pool_tmp, plain=True)
        norm_mlp = [Norm("nm0", 2, ready=(mixed, NC * KT)), Norm("nm1", 3, ready=(o_added, NC * KT))]
        norm_q = Norm("nq", 5, ready=(m_added[0], NC * KT * NG))
        norm_kv = Norm("nkv", 4, stats=False, ready=(norm_q.lo, NC), free=(w_used, n_of["k"]))

        class Mlp:
            def __init__(self, l):
                self.l, self.n0, self.norm = l, n_of[f"mlp{l}"], norm_mlp[l]
                name = f"m{l}"
                self.up_full, self.relu, self.sq, self.hi, self.lo = (sem(name + s) for s in ("uf", "re", "sq", "hi", "lo"))
                self.down_full, self.added = sem(name + "df"), m_added[l]

            def pe(self, pe):
                def up(g, first):
                    for j in range(GT):
                        pe.wait_ge(w_split, (g * (4 * GT) + (2 * (self.n0 + j + 1) - 2 * GT)) if not (first and g == 0)
                                   else 2 * (self.n0 + j + 1))
                        for c in range(NC):
                            if first and g == 0 and j == 0:
                                pe.wait_ge(self.norm.lo, c + 1)
                            if j >= 2:
                                pe.wait_ge(self.relu, g * (3 * GT) + (3 * (j - 2) + c + 1))
                            elif first and g == 1:
                                pe.wait_ge(self.relu, 3 * (GT - 2 + j) + c + 1)
                            elif not first:
                                pe.wait_ge(self.added, g * (3 * KT) + (-3 * KT + 3 * (-2 + j) + c + 1))
                            last = products(pe, j % 2, 0, KT, c, NC * (j % 2) + c, xh, xl,
                                            frees=(c == 0 and not (first and g == 0 and j == 0)))
                            last.then_inc(self.up_full, 1)
                def down(g, slot):
                    pe.wait_ge(self.lo, g * (3 * GT) + 3 * GT)
                    for dm in range(KT):
                        par = (dm // 2) % 2
                        if dm % 2 == 0:
                            pe.wait_ge(w_split, nd(g, dm // 2) * 2 + 2)
                        for c in range(NC):
                            if dm < 2:
                                if isinstance(g, int) and g == NG - 1:
                                    pe.wait_ge(self.added, 3 * KT * (NG - 1) - 6 + 3 * dm + c + 1)
                                else:
                                    pe.wait_ge(self.relu, g * (3 * GT) + (3 * GT + 3 * (2 + dm) + c + 1))
                            else:
                                pe.wait_ge(self.added, g * (3 * KT) + (3 * (dm - 2) + c + 1))
                            for k in range(GT):
                                at_ = k * 2 * P + (dm % 2) * P
                                wh, wl = w_hi[:, par, at_:at_ + P], w_lo[:, par, at_:at_ + P]
                                hh, hl = hidden(g, k, c)
                                for i, (w, x) in enumerate(((wl, hh), (wh, hl), (wh, hh))):
                                    last = pe.matmul(ps[:, NC * (dm % 2) + c, 0:CH], w, x,
                                                     start=(k == 0 and i == 0), stop=(k == GT - 1 and i == 2))
                                    if dm % 2 == 0 and c == 0 and k == 0 and i == 0:
                                        last.then_inc(w_used, 1)
                            last.then_inc(self.down_full, 1)
                def nd(g, q):
                    if isinstance(g, int):
                        return self.n0 + (2 * GT * (g + 1) + q if g < NG - 1 else 2 * GT * NG - GT + q)
                    return g * (2 * GT) + (self.n0 + 2 * GT + q)
                def hidden(g, k, c):
                    return (hid_hi[:, self.half * GT + k, chunk(c)], hid_lo[:, self.half * GT + k, chunk(c)])
                self.two_a_turn(pe, up, down)
                pe.drain().then_inc(w_used, 1)

            def two_a_turn(self, eng, up, down):
                up(0, True)
                self.half = 0
                self.uhalf = 1
                up(1, True)
                down(0, 0)
                with eng.Fori(0, (NG - 2) // 2, 1) as i:
                    for odd in range(2):
                        self.uhalf = odd
                        up(i * 2 + (2 + odd), False)
                        self.half = 1 - odd
                        down(i * 2 + (1 + odd), None)
                self.half = (NG - 1) % 2
                down(NG - 1, None)

            def act(self, act):
                def up(g, first):
                    for j in range(GT):
                        for c in range(NC):
                            act.wait_ge(self.up_full, g * (3 * GT) + (3 * j + c + 1))
                            if not (first and g == 0 and j == 0):
                                act.wait_ge(self.sq, g * (3 * GT) + (3 * (j - 1) + c + 1))
                            act.activation(tmp_a[:, c, :], ps[:, NC * (j % 2) + c, 0:CH], ACT.Relu).then_inc(self.relu, 1)
                        for c in range(NC):
                            act.wait_ge(self.sq, g * (3 * GT) + (3 * j + c + 1))
                            act.activation(hid_hi[:, self.uhalf * GT + j, chunk(c)], tmp_b[:, c, :],
                                           ACT.Copy).then_inc(self.hi, 1)
                self.uhalf = 0
                self.two_a_turn(act, up, lambda g, s: None)

            def dve(self, dve):
                def up(g, first):
                    for j in range(GT):
                        for c in range(NC):
                            dve.wait_ge(self.relu, g * (3 * GT) + (3 * j + c + 1))
                            if not (first and g == 0 and j == 0):
                                dve.wait_ge(self.lo, g * (3 * GT) + (3 * (j - 1) + c + 1))
                            dve.tensor_tensor(tmp_b[:, c, :], tmp_a[:, c, :], tmp_a[:, c, :], ALU.mult).then_inc(self.sq, 1)
                        for c in range(NC):
                            dve.wait_ge(self.hi, g * (3 * GT) + (3 * j + c + 1))
                            dve.tensor_tensor(hid_lo[:, self.uhalf * GT + j, chunk(c)], tmp_b[:, c, :],
                                              hid_hi[:, self.uhalf * GT + j, chunk(c)].bitcast(F32),
                                              ALU.subtract).then_inc(self.lo, 1)
                def down(g, slot):
                    for dm in range(KT):
                        for c in range(NC):
                            dve.wait_ge(self.down_full, g * (3 * KT) + (3 * dm + c + 1))
                            if not (isinstance(g, int) and g == 0):
                                dve.wait_ge(self.added, g * (3 * KT) + (3 * dm + c + 1 - 3 * KT))
                            dve.tensor_tensor(h[:, dm, chunk(c)], ps[:, NC * (dm % 2) + c, 0:CH],
                                              h[:, dm, chunk(c)], ALU.add).then_inc(self.added, 1)
                self.uhalf = 0
                self.two_a_turn(dve, up, down)

        mlps = [Mlp(0), Mlp(1)]

        class Proj:
            def __init__(self, name, x_ready, norm=False, store=None, copied=None):
                self.name, self.n0, self.x_ready = name, n_of[name], x_ready
                self.norm, self.store = norm, store
                (self.full, self.copied, self.sq, self.sum, self.root, self.rec, self.done, self.tr, self.ev,
                 self.kept, self.sent) = (sem(f"p{name}_{s}") if self.needs(s) else None for s in
                                     ("full", "cp", "sq", "sum", "root", "rec", "done", "tr", "ev", "kept", "sent"))
                if copied is not None:
                    self.copied = copied

            def needs(self, s):
                return (s == "full" or (s == "cp" and self.name != "o")
                        or (s in ("sq", "sum", "root", "rec", "done") and bool(self.norm))
                        or (s in ("tr", "ev", "sent") and bool(self.store))
                        or (s == "kept" and bool(self.norm) and bool(self.store)))

            def pe(self, pe):
                def main(m, par, first):
                    pe.wait_ge(w_split, m * 2 + (2 * self.n0 + 2))
                    for c in range(NC):
                        if first:
                            if par == 0:
                                pe.wait_ge(*self.x_ready(c))
                        else:
                            pe.wait_ge(self.copied, m * 3 + (c + 1 - 6))
                        last = products(pe, par, 0, KT, c, NC * par + c, xh, xl,
                                        frees=(c == 0 and not (first and par == 0)))
                        last.then_inc(self.full, 1)

                def sums(m, first):
                    if self.norm:
                        for c in range(NC):
                            pe.wait_ge(self.sq, m * 3 + (c + 1))
                            if c == 2:
                                pe.wait_ge(self.root, m * 3 + 1)
                            elif self.store and not first:
                                pe.wait_ge(self.ev, m * 3)
                            elif not self.store and not first:
                                pe.wait_ge(self.root, m * 3)
                            pe.matmul(ps[:, 6 + c % 2, 0:CH], block_ones[:, :], tmp_b[:, c, :], start=True,
                                      stop=True).then_inc(self.sum, 1)

                def turn(m, first):
                    if self.store:
                        for b in range(3):
                            if b == 0:
                                pe.wait_ge(self.done if self.norm else self.copied, m * 3 + 3)
                                if not self.norm and not first:
                                    pe.wait_ge(self.ev, m * 3)
                                if self.norm:
                                    pe.wait_ge(self.root, m * 3 + 3)
                            if b == 2:
                                pe.wait_ge(self.ev, m * 3 + 1)
                            src = tmp_a[:, :, :].rearrange("p c t -> p (c t)")
                            for t in range(4 * b, min(4 * b + 4, NTT)):
                                w = min(P, N - t * P)
                                last = pe.transpose(ps[0:w, 6 + b % 2, (t % 4) * P:(t % 4) * P + P],
                                                    src[:, t * P:t * P + w], ident[:, :])
                            last.then_inc(self.tr, 1)
                def after(m, first):
                    if self.store:
                        turn(m - 1, first)
                        sums(m, False)
                    else:
                        sums(m - 1, first)
                main(0, 0, True)
                if self.store:
                    sums(0, True)
                main(1, 1, True)
                after(1, True)
                with pe.Fori(1, KT // 2, 1) as i:
                    for j in range(2):
                        main(i * 2 + j, j, False)
                        after(i * 2 + j, False)
                pe.drain().then_inc(w_used, 1)
                if self.store:
                    turn(KT - 1, False)
                else:
                    sums(KT - 1, False)

            def tiles(self, eng, one):
                one(0, 0, True)
                one(1, 1, False)
                with eng.Fori(1, KT // 2, 1) as i:
                    for j in range(2):
                        one(i * 2 + j, j, False)

            def act(self, act):
                def one(m, par, first):
                    for c in range(NC):
                        act.wait_ge(self.full, m * 3 + (c + 1))
                        if first and self.name == "v":
                            act.wait_ge(proj_k.tr, 3 * KT)
                            act.wait_ge(proj_k.kept, KT)
                        if not first:
                            if self.store:
                                act.wait_ge(self.tr, m * 3)
                                if self.norm:
                                    act.wait_ge(self.kept, m)
                            elif self.norm:
                                act.wait_ge(self.done, m * 3 + (c + 1 - 3))
                        act.activation(tmp_a[:, c, :], ps[:, NC * par + c, 0:CH], ACT.Copy).then_inc(self.copied, 1)
                    if self.norm:
                        for c in range(NC):
                            act.wait_ge(self.sum, m * 3 + (c + 1))
                            act.activation(tmp_b[:, c, :], ps[:, 6 + c % 2, 0:CH], ACT.Sqrt, bias=eps_c[:, 0:1],
                                           scale=1.0 / HD).then_inc(self.root, 1)
                    if self.store:
                        for b in range(3):
                            act.wait_ge(self.tr, m * 3 + (b + 1))
                            if b == 0:
                                if not first:
                                    act.wait_ge(self.sent, m * 32)
                                elif self.name == "v":
                                    act.wait_ge(proj_k.sent, 32 * KT)
                                else:
                                    act.wait_ge(st_out, 16 * 2)
                            nt = min(4, NTT - 4 * b)
                            w = P if b < 2 else S
                            act.activation(o_tok[0:w, 4 * b:4 * b + nt, :],
                                           ps[0:w, 6 + b % 2, 0:nt * P].rearrange("p (t c) -> p t c", c=P),
                                           ACT.Copy).then_inc(self.ev, 1)
                        act.wait_ge(self.ev, m * 3 + 3)
                        dst_p, dst_s = self.store
                        act.dma_start(dst_p[bass.ds(m, 1)].rearrange("o p t c -> (o p) t c"),
                                      o_tok[:, 0:NQ, :]).then_inc(self.sent, 16)
                        act.dma_start(dst_s[bass.ds(m, 1)].rearrange("o p c -> (o p) c"),
                                      o_tok[0:S, NQ, :]).then_inc(self.sent, 16)
                self.tiles(act, one)

            def dve(self, dve):
                if not self.norm:
                    return
                gain, out = self.norm

                def one(m, par, first):
                    for c in range(NC):
                        dve.wait_ge(self.copied, m * 3 + (c + 1))
                        if not first:
                            dve.wait_ge(self.done, m * 3)
                        dve.tensor_tensor(tmp_b[:, c, :], tmp_a[:, c, :], tmp_a[:, c, :], ALU.mult).then_inc(self.sq, 1)
                    for c in range(NC):
                        dve.wait_ge(self.root, m * 3 + (c + 1))
                        dve.reciprocal(tmp_b[:, c, :], tmp_b[:, c, :]).then_inc(self.rec, 1)
                        dve.wait_ge(self.rec, m * 3 + (c + 1))
                        o = tmp_a[:, c, :] if self.store else out[:, bass.ds(m, 1), chunk(c)].rearrange("p o t -> p (o t)")
                        dve.scalar_tensor_tensor(o, tmp_a[:, c, :], gain, tmp_b[:, c, :], ALU.mult,
                                                 ALU.mult).then_inc(self.done, 1)
                self.tiles(dve, one)

            def pool(self, pool):
                out = self.norm[1]

                def keep(m):
                    pool.wait_ge(self.done, m * 3 + 3)
                    apart(pool)
                    pool.tensor_copy(out[:, bass.ds(m, 1), :].rearrange("p o t -> p (o t)"),
                                     tmp_a[:, :, :].rearrange("p c t -> p (c t)")).then_inc(self.kept, 1)
                return keep

        def rows(x_p, x_s):
            return (x_p[0].rearrange("(t p) h d -> p t (h d)", p=P).rearrange("p t (m c) -> m p t c", c=P),
                    x_s.rearrange("b t h d -> (b t) (h d)").rearrange("p (m c) -> m p c", c=P))

        proj_q = Proj("q", lambda c: (norm_q.lo, c + 1), norm=(gains[:, 2:3], qT))
        proj_k = Proj("k", lambda c: (norm_kv.lo, c + 1), norm=(gains[:, 1:2], kT), store=rows(k_p, k_s))
        proj_v = Proj("v", lambda c: (norm_kv.lo, c + 1), store=rows(v_p, v_s))
        o_split_hi, o_split_lo = sem("o_split_hi"), sem("o_split_lo")
        proj_o = Proj("o", lambda c: (o_split_lo, c + 1), copied=o_added)

        s_vec, s_par, s_x, s_pre = sem("s_vec"), sem("s_par"), [sem("s_x0"), sem("s_x1")], sem("s_pre")
        vec_tr, vec_cp, x_tr, x_cp, pre_tr, pre_cp = (sem(n) for n in
            ("vec_tr", "vec_cp", "x_tr", "x_cp", "pre_tr", "pre_cp"))
        ext_done, win_done, pooled, pool_hi, pool_lo, mix_full = (sem(n) for n in
            ("ext_done", "win_done", "pooled", "pool_hi", "pool_lo", "mix_full"))
        st_tr, st_cp, cnt_done, zeroed = sem("st_tr"), sem("st_cp"), sem("cnt_done"), sem("zeroed")
        f_full, f_act, f_dve, f_tr, f_cp = (sem(n) for n in ("f_full", "f_act", "f_dve", "f_tr", "f_cp"))
        (s_in, s_pg, s_vg, k_tr, k_ev, sd_prep, s_full, s_max, s_neg, s_exp, s_rec, s_nrm, p_tr, p_ev,
         a_full, a_ev, s_const, s_cc) = (sem("sa_" + n) for n in
            ("in", "pg", "vg", "ktr", "kev", "prep", "full", "max", "neg", "exp", "rec", "nrm", "ptr", "pev",
             "afull", "aev", "const", "cc"))
        (c_done, c_sent, r_in, v_in, aug, q_full, q_max, q_neg, q_exp, q_rec, q_nrm, t_full, t_ev,
         o_full, o_ev, a_const) = (sem("pa_" + n) for n in
            ("c", "csent", "rin", "vin", "aug", "full", "max", "neg", "exp", "rec", "nrm", "tr", "tev",
             "ofull", "oev", "const"))
        one_rows = sem("pa_ones")
        v_in2, r_in2 = sem("pa_vin2"), sem("pa_rin2")
        y_tr, y_cp, y_out, lf_out, st_out = sem("y_tr"), sem("y_cp"), [sem("y_out0"), sem("y_out1")], sem("lf_out"), sem("st_out")

        x_src = [x_prompt[0, t * P:(t + 1) * P, :] for t in range(NQ)] + [x_sample.rearrange("b t d -> (b t) d")]

        def ext_cols(k, kind):
            e = ext[:, k, :] if isinstance(k, int) else ext[:, k[0]:k[1], :]
            if kind == "p":
                return e[..., BUF:BUF + T]
            return e[..., BUF + T:].rearrange("p (b e) -> p b e", e=EXT)[..., BUF:]

        block = ctx.enter_context(nc.Block())

        def sample_pool(pool):
            pool.wait_ge(w_used, n_of["v"] + KT)
            pool.memset(q_bd[:, :], 0.0).then_inc(s_const, 1)
            pool.memset(after[:, :, :], 1.0).then_inc(s_const, 1)
            pool.memset(own[:, :, :, :], 1.0).then_inc(s_const, 1)
            pool.wait_ge(s_const, 3)
            pool.affine_select(out=after[:, 0, 0:P], in_=after[:, 0, 0:P], compare_op=ALU.is_gt, fill=0.0, base=0,
                               pattern=[[-1, P]], channel_multiplier=1).then_inc(s_const, 1)
            pool.memset(after[:, 0, P:NKEY], 0.0).then_inc(s_const, 1)
            pool.affine_select(out=after[:, 1, P:2 * P], in_=after[:, 1, P:2 * P], compare_op=ALU.is_gt, fill=0.0,
                               base=0, pattern=[[-1, P]], channel_multiplier=1).then_inc(s_const, 1)
            pool.memset(after[:, 1, 2 * P:NKEY], 0.0).then_inc(s_const, 1)
            pool.affine_select(out=after[:, 2, 2 * P:NKEY], in_=after[:, 2, 2 * P:NKEY], compare_op=ALU.is_gt,
                               fill=0.0, base=0, pattern=[[-1, S]], channel_multiplier=1).then_inc(s_const, 1)
            flat = own[:, :, :, :]
            pool.affine_select(out=flat, in_=flat, compare_op=ALU.is_ge, fill=0.0, base=0,
                               pattern=[[-TS, NB], [0, NH], [0, TS]], channel_multiplier=1).then_inc(s_const, 1)
            pool.wait_ge(s_const, 9)
            pool.affine_select(out=flat, in_=flat, compare_op=ALU.is_ge, fill=0.0, base=0,
                               pattern=[[TS, NB], [0, NH], [1, TS]], channel_multiplier=-1).then_inc(s_const, 1)

        def sample_sp(sp):
            sp.wait_ge(s_par, 16 * 7)
            sp.wait_ge(w_used, n_of["v"] + KT)
            sp.wait_ge(proj_v.sent, 32 * KT)
            sp.dma_start(v_new[:, :], v_s.rearrange("b t h d -> (b t) (h d)")).then_inc(s_in, 16)
            def sequence(b):
                pages = [sp.value_load(pt_sb[0:1, bass.ds(b * 2 + g, 1)], min_val=0, max_val=NPOOL - 1) for g in range(2)]
                wait_past(sp, s_full, b)
                for g, page in enumerate(pages):
                    sp.dma_start(k_pg[:, g, :], cache_k[bass.ds(page, 1)].rearrange("o p h d -> (o p) (h d)")).then_inc(s_pg, 16)
                    sp.dma_start(lf_pg[:, g, :], cache_logf[bass.ds(page, 1)].rearrange("o p h -> (o p) h")).then_inc(s_pg, 16)
                wait_past(sp, a_full, b)
                for g, page in enumerate(pages):
                    sp.dma_start(v_pg[:, g, :], cache_v[bass.ds(page, 1)].rearrange("o p h d -> (o p) (h d)")).then_inc(s_vg, 16)
            sequence(0)
            with sp.Fori(1, NB, 1) as b:
                sequence(b)

        def sample_pe(pe):
            def sequence(b):
                pe.wait_ge(s_pg, b * 64 + 64)
                wait_past(pe, k_ev, b * 4)
                for quad in range(4):
                    g, p0 = quad // 2, 4 * (quad % 2)
                    for p in range(p0, p0 + 4):
                        last = pe.transpose(ps[:, quad, (p - p0) * P:(p - p0 + 1) * P], k_pg[:, g, p * P:(p + 1) * P],
                                            ident[:, :])
                    last.then_inc(k_tr, 1)
                pe.wait_ge(k_ev, b * 4 + 4)
                pe.wait_ge(sd_prep, b * 6 + 6)
                pe.wait_ge(s_const, 10)
                pe.wait_ge(s_cc, 2)
                wait_past(pe, s_exp, b)
                for p in range(KT):
                    pe.matmul(ps[0:R, 4, 0:NKEY], q_bd[:, p * R:(p + 1) * R], kTa[:, p, :], start=(p == 0),
                              stop=False)
                for g in range(2):
                    pe.matmul(ps[0:R, 4, 0:NKEY], lf_pb[:, g, :, :].rearrange("p h t -> p (h t)"), after[:, g, :],
                              start=False, stop=False)
                pe.matmul(ps[0:R, 4, 0:NKEY], lf_new[:, :, :].rearrange("p h t -> p (h t)"), after[0:S, 2, :],
                          start=False, stop=False)
                pe.matmul(ps[0:R, 4, 2 * P:NKEY], neg_b[:, :, :].rearrange("p h t -> p (h t)"), ident[0:S, 0:S],
                          start=False, stop=True).then_inc(s_full, 1)
                pe.wait_ge(s_nrm, b + 1)
                wait_past(pe, p_ev, b * 2)
                apart(pe)
                for g in range(3):
                    w = P if g < 2 else S
                    last = pe.transpose(ps[0:w, 5, g * R:(g + 1) * R], p_s[:, g * P:g * P + w], ident[0:R, 0:R])
                last.then_inc(p_tr, 1)
                pe.wait_ge(p_ev, b * 2 + 2)
                pe.wait_ge(s_vg, b * 32 + 32)
                pe.wait_ge(s_in, 16)
                wait_past(pe, a_ev, b * 2)
                for p in range(KT):
                    for g in range(3):
                        v = v_pg[:, g, p * P:(p + 1) * P] if g < 2 else v_new[:, p * P:(p + 1) * P]
                        w = P if g < 2 else S
                        last = pe.matmul(ps[:, 6, 8 * p:8 * p + 8], v, pT_s[0:w, g, 8 * p:8 * p + 8],
                                         start=(g == 0), stop=(g == 2))
                last.then_inc(a_full, 1)
            sequence(0)
            with pe.Fori(1, NB, 1) as b:
                sequence(b)

        def sample_act(act):
            def sequence(b):
                for quad in range(4):
                    g, p0 = quad // 2, 4 * (quad % 2)
                    act.wait_ge(k_tr, b * 4 + (quad + 1))
                    act.activation(kTa[:, p0:p0 + 4, g * P:(g + 1) * P],
                                   ps[:, quad, :].rearrange("p (t c) -> p t c", c=P), ACT.Copy).then_inc(k_ev, 1)
                act.wait_ge(s_neg, b + 1)
                wait_past(act, p_tr, b)
                act.activation(p_s[:, :], ps[0:R, 4, 0:NKEY], ACT.Exp, bias=small[0:R, 1:2],
                               accum_out=small[0:R, 2:3]).then_inc(s_exp, 1)
            sequence(0)
            with act.Fori(1, NB, 1) as b:
                sequence(b)

        def sample_dve(dve):
            dve.wait_ge(w_used, n_of["v"] + KT)
            dve.wait_ge(proj_k.kept, KT)
            dve.tensor_copy(kTa[:, :, 2 * P:NKEY], kT[:, :, T:N]).then_inc(s_cc, 1)
            dve.wait_ge(s_const, 10)
            dve.tensor_scalar(own_neg[:, :, :, :], own[:, :, :, :], -1.0, BIG, ALU.add, ALU.mult).then_inc(s_cc, 1)
            dve.wait_ge(s_cc, 2)
            def sequence(b):
                wait_past(dve, s_full, b)
                dve.wait_ge(s_pg, b * 64 + 64)
                apart(dve)
                even = q_bd[0:HD, :].rearrange("p (k s) -> p k s", s=72)[:, :, 0:TS]
                odd = q_bd[HD:P, :].rearrange("p (k s) -> p k s", s=72)[:, :, TS:2 * TS]
                dve.tensor_copy(even, qT[0:HD, :, bass.ds(b * TS + T, TS)]).then_inc(sd_prep, 1)
                dve.tensor_copy(odd, qT[HD:P, :, bass.ds(b * TS + T, TS)]).then_inc(sd_prep, 1)
                for g in range(2):
                    dve.tensor_copy(lf_pb[:, g, :, :], lf_pg[:, g, :].unsqueeze(2).to_broadcast([P, NH, TS])).then_inc(sd_prep, 1)
                dve.tensor_tensor(lf_new[:, :, :], own[:, bass.ds(b, 1), :, :].rearrange("p o h t -> p (o h) t"),
                                  lfT[0:S, NQ, :].unsqueeze(2).to_broadcast([S, NH, TS]), ALU.mult).then_inc(sd_prep, 1)
                dve.tensor_copy(neg_b[:, :, :], own_neg[:, bass.ds(b, 1), :, :].rearrange("p o h t -> p (o h) t")).then_inc(sd_prep, 1)
                dve.wait_ge(s_full, b + 1)
                dve.tensor_reduce(small[0:R, 0:1], ps[0:R, 4, 0:NKEY], AX, ALU.max).then_inc(s_max, 1)
                dve.wait_ge(s_max, b + 1)
                dve.tensor_scalar(small[0:R, 1:2], small[0:R, 0:1], -1.0, None, ALU.mult).then_inc(s_neg, 1)
                dve.wait_ge(s_exp, b + 1)
                dve.reciprocal(small[0:R, 3:4], small[0:R, 2:3]).then_inc(s_rec, 1)
                dve.wait_ge(s_rec, b + 1)
                dve.tensor_scalar(p_s[:, :], p_s[:, :], small[0:R, 3:4], None, ALU.mult).then_inc(s_nrm, 1)
                dve.wait_ge(p_tr, b + 1)
                dve.tensor_copy(pT_s[:, 0:2, :], ps[:, 5, 0:2 * R].rearrange("p (g r) -> p g r", g=2)).then_inc(p_ev, 1)
                dve.tensor_copy(pT_s[0:S, 2, :], ps[0:S, 5, 2 * R:3 * R]).then_inc(p_ev, 1)
                dve.wait_ge(a_full, b + 1)
                apart(dve)
                o = ps[:, 6, 0:R].rearrange("p (k s) -> p k s", s=2 * TS)
                dve.tensor_copy(qT[0:HD, :, bass.ds(b * TS + T, TS)], o[0:HD, :, 0:TS]).then_inc(a_ev, 1)
                dve.tensor_copy(qT[HD:P, :, bass.ds(b * TS + T, TS)], o[HD:P, :, TS:2 * TS]).then_inc(a_ev, 1)
            sequence(0)
            with dve.Fori(1, NB, 1) as b:
                sequence(b)

        NP = NH // 2

        def pairs(eng, body):
            body(0, False)
            with eng.Fori(1, NP - 1, 1) as r:
                body(r, False)
            body(NP - 1, True)

        def prompt_sp(sp):
            sp.wait_ge(a_ev, 2 * NB)
            sp.wait_ge(one_rows, 4)
            sp.wait_ge(c_done, 2)
            sp.dma_start(cum_dram[0], cum[:, :]).then_inc(c_sent, 16)
            sp.dma_start(cum_dram[1], ncum[:, :]).then_inc(c_sent, 16)
            sp.wait_ge(c_sent, 32)
            vv = v_p[0].rearrange("(t p) h d -> h p t d", p=P)
            rs = [(r_in, v_in), (r_in2, v_in2)]

            def head(r, e):
                hh = r * 2 + e
                sp.dma_start(q_aug[e][HD:HD + 1, :], cum_dram[0][bass.ds(hh, 1), :]).then_inc(rs[e][0], 16)
                sp.dma_start(k_aug[e][HD + 1:HD + 2, :], cum_dram[1][bass.ds(hh, 1), :]).then_inc(rs[e][0], 16)

            def values(r, e):
                hh = r * 2 + e
                sp.dma_start(v_h[e][:, :, :], vv[bass.ds(hh, 1)].rearrange("o p t d -> (o p) t d")).then_inc(rs[e][1], 16)
            for e in range(2):
                head(0, e)
                values(0, e)
            with sp.Fori(0, NP - 1, 1) as r:
                for e in range(2):
                    sp.wait_ge(q_full, r * (2 * NQ) + NQ * (e + 1))
                    head(r + 1, e)
                    sp.wait_ge(o_full, r * 4 + 2 * (e + 1))
                    values(r + 1, e)

        def prompt_pe(pe):
            def body(r, last_pair):
                def score(l):
                    e, i = divmod(l, NQ)
                    if i == 0:
                        pe.wait_ge(aug, r * 4 + 2 * (e + 1))
                        pe.wait_ge([r_in, r_in2][e], r * 32 + 32)
                    b = 2 * (l % 2)
                    wait_past(pe, q_exp, r * 16 + max(0, l - 1))
                    n = (i + 1) * P
                    q = q_aug[e][0:HD + 2, i * P:n]
                    for s in range(0, n, 512):
                        w = min(512, n - s)
                        pe.matmul(ps[:, b + s // 512, 0:w], q, k_aug[e][0:HD + 2, s:s + w], start=True,
                                  stop=(s + w < n))
                    at_ = i * P % 512
                    pe.matmul(ps[:, b + i * P // 512, at_:at_ + P], ident_b[:, :], causal_b[:, :], start=False,
                              stop=True).then_inc(q_full, 1)

                def turn(l):
                    e, i = divmod(l, NQ)
                    pe.wait_ge(q_nrm, r * 16 + (l + 1))
                    for s in range(0, i + 1, 4):
                        wait_past(pe, t_ev, r * 24 + max(0, quads_before(l) + s // 4 - 1))
                        bank = 4 + (quads_before(l) + s // 4) % 2
                        for kb in range(s, min(s + 4, i + 1)):
                            last = pe.transpose(ps[:, bank, (kb - s) * P:(kb - s + 1) * P],
                                                probs[l % 2][:, kb * P:(kb + 1) * P], ident[:, :])
                        last.then_inc(t_full, 1)

                def weigh(e, g):
                    n_av = 2 * e + g
                    pe.wait_ge(t_ev, r * 24 + quads_before(NQ * e + 4 * g + 4))
                    pe.wait_ge([v_in, v_in2][e], r * 16 + 16)
                    wait_past(pe, o_ev, r * 4 + max(0, n_av - 1))
                    for kb in range(4 * g + 4):
                        lo = max(0, kb - 4 * g) * P
                        last = pe.matmul(ps[0:HD, 6 + n_av % 2, lo:512], v_h[e][:, kb, :], probsT[:, kb, lo:512],
                                         start=(kb == 0), stop=(kb == 4 * g + 3))
                    last.then_inc(o_full, 1)
                score(0)
                score(1)
                for l in range(2 * NQ):
                    turn(l)
                    if l + 2 < 2 * NQ:
                        score(l + 2)
                    if l % 4 == 3:
                        weigh(l // NQ, (l % NQ) // 4)
            pairs(pe, body)

        def quads_before(l):
            return sum((i % NQ) // 4 + 1 for i in range(l))

        def prompt_act(act):
            def body(r, last_pair):
                def exp(l):
                    e, i = divmod(l, NQ)
                    n = (i + 1) * P
                    act.wait_ge(q_neg, r * 16 + (l + 1))
                    wait_past(act, t_full, r * 24 + quads_before(max(0, l - 1)))
                    act.activation(probs[l % 2][:, 0:n],
                                   ps[:, 2 * (l % 2):2 * (l % 2) + 2, :].rearrange("p b n -> p (b n)")[:, 0:n],
                                   ACT.Exp, bias=stat[:, 1, l % 2:l % 2 + 1],
                                   accum_out=stat[:, 2, l % 2:l % 2 + 1]).then_inc(q_exp, 1)

                def turned(l):
                    e, i = divmod(l, NQ)
                    for s in range(0, i + 1, 4):
                        nq = quads_before(l) + s // 4
                        act.wait_ge(t_full, r * 24 + (nq + 1))
                        av = l // 4
                        wait_past(act, o_full, r * 4 + av)
                        nb = min(4, i + 1 - s)
                        act.activation(probsT[:, s:s + nb, (i % 4) * P:(i % 4 + 1) * P],
                                       ps[:, 4 + nq % 2, 0:nb * P].rearrange("p (b c) -> p b c", c=P),
                                       ACT.Copy).then_inc(t_ev, 1)
                exp(0)
                exp(1)
                for l in range(2 * NQ):
                    turned(l)
                    if l + 2 < 2 * NQ:
                        exp(l + 2)
            pairs(act, body)

        def prompt_dve(dve):
            dve.wait_ge(a_ev, 2 * NB)
            dve.wait_ge(a_const, 1)
            dve.tensor_tensor_scan(cum[:, :], lf_row[:, 0:T], zero_r[:, :], 0.0, ALU.add, ALU.add).then_inc(c_done, 1)
            for e in range(2):
                dve.memset(q_aug[e][HD:HD + 2, :], 1.0).then_inc(one_rows, 1)
                dve.memset(k_aug[e][HD:HD + 2, :], 1.0).then_inc(one_rows, 1)
            dve.wait_ge(c_done, 1)
            dve.tensor_scalar(ncum[:, :], cum[:, :], -1.0, None, ALU.mult).then_inc(c_done, 1)

            def build(r, e, used):
                if used is not None:
                    dve.wait_ge(q_full, used)
                    apart(dve)
                half = slice(HD * e, HD * e + HD)
                dve.tensor_copy(q_aug[e][0:HD, :], qT[half, bass.ds(r, 1), 0:T].rearrange("p o t -> p (o t)")).then_inc(aug, 1)
                dve.tensor_copy(k_aug[e][0:HD, :], kT[half, bass.ds(r, 1), 0:T].rearrange("p o t -> p (o t)")).then_inc(aug, 1)
            build(0, 0, None)
            build(0, 1, None)

            def body(r, last_pair):
                def top(l):
                    e, i = divmod(l, NQ)
                    n = (i + 1) * P
                    dve.wait_ge(q_full, r * 16 + (l + 1))
                    dve.tensor_reduce(stat[:, 0, l % 2:l % 2 + 1],
                                      ps[:, 2 * (l % 2):2 * (l % 2) + 2, :].rearrange("p b n -> p (b n)")[:, 0:n],
                                      AX, ALU.max).then_inc(q_max, 1)
                    dve.wait_ge(q_max, r * 16 + (l + 1))
                    dve.tensor_scalar(stat[:, 1, l % 2:l % 2 + 1], stat[:, 0, l % 2:l % 2 + 1], -1.0, None,
                                      ALU.mult).then_inc(q_neg, 1)

                def inv(l):
                    dve.wait_ge(q_exp, r * 16 + (l + 1))
                    wait_past(dve, q_nrm, r * 16 + max(0, l - 1))
                    dve.reciprocal(stat[:, 3, l % 2:l % 2 + 1], stat[:, 2, l % 2:l % 2 + 1]).then_inc(q_rec, 1)
                    n = (l % NQ + 1) * P
                    dve.wait_ge(q_rec, r * 16 + (l + 1))
                    dve.tensor_scalar(probs[l % 2][:, 0:n], probs[l % 2][:, 0:n], stat[:, 3, l % 2:l % 2 + 1], None,
                                      ALU.mult).then_inc(q_nrm, 1)

                def out(e, g):
                    n_av = 2 * e + g
                    dve.wait_ge(o_full, r * 4 + (n_av + 1))
                    apart(dve)
                    dve.tensor_copy(qT[HD * e:HD * e + HD, bass.ds(r, 1), 512 * g:512 * g + 512].rearrange("p o t -> p (o t)"),
                                    ps[0:HD, 6 + n_av % 2, :]).then_inc(o_ev, 1)
                top(0)
                top(1)
                inv(0)
                for l in range(2 * NQ):
                    if l + 1 < 2 * NQ:
                        inv(l + 1)
                    if l + 2 < 2 * NQ:
                        top(l + 2)
                    if l % 4 == 3:
                        out(l // NQ, (l % NQ) // 4)
                    if l % NQ == NQ - 1 and not last_pair:
                        build(r + 1, l // NQ, r * 16 + (l + 1))
            pairs(dve, body)

        def prompt_pool(pool):
            pool.wait_ge(a_ev, 2 * NB)
            pool.memset(zero_r[:, :], 0.0).then_inc(a_const, 1)
            pool.tensor_copy(ident_b[:, :], ident[:, :]).then_inc(a_const, 1)
            pool.memset(causal_b[:, :], 0.0).then_inc(a_const, 1)
            pool.wait_ge(a_const, 3)
            pool.affine_select(out=causal_b[:, :], in_=causal_b[:, :], compare_op=ALU.is_ge, fill=-BIG, base=0,
                               pattern=[[-1, P]], channel_multiplier=1).then_inc(a_const, 1)

        def norm_pool_squares(act):
            for n in range(2 * NTT):
                t, b = divmod(n, 2)
                w = min(P, N - t * P)
                act.wait_ge(x_tr, n + 1)
                act.activation(h[:, 4 * b:4 * b + 4, t * P:t * P + w],
                               ps[:, n % 4, :].rearrange("p (k c) -> p k c", c=P)[:, :, 0:w], ACT.Copy).then_inc(x_cp, 1)
                if t == 1 and b == 1:
                    act.wait_ge(vec_tr, 1)
                    act.activation(vecs[:, :], ps[:, 4, 0:6 * KT], ACT.Copy).then_inc(vec_cp, 1)
                    act.wait_ge(const_ready, 9)
                    for q in range(2):
                        act.wait_ge(pre_tr, q + 1)
                        for k in range(4):
                            act.activation(ext[:, 4 * q + k, BUF + T:].rearrange("p (b e) -> p b e", e=EXT)[:, :, 0:BUF],
                                           ps[:, 5 + q, k * P:k * P + NB * BUF].rearrange("p (b e) -> p b e", e=BUF),
                                           ACT.Copy).then_inc(pre_cp, 1)
            act.wait_ge(x_cp, 2 * NTT)
            norm_pool.act(act)

        @block.sync
        def _(sp):
            for t in range(NTT):
                if t >= 2:
                    sp.wait_ge(x_tr, 2 * (t - 1))
                w = P if t < NQ else S
                sp.dma_start(x_tok[0:w, t % 2, :], x_src[t]).then_inc(s_x[t % 2], 16)
                if t == 1:
                    for i, v in enumerate((ins["g_pool"][0], ins["pool_scale"][0], ins["g_mlp"][0], ins["g_mlp"][1],
                                           ins["g_kv"], ins["g_attn"][0])):
                        sp.dma_start(vec_rows[i * KT:(i + 1) * KT, :], v.rearrange("(k p) -> k p", p=P)).then_inc(s_vec, 16)
                    sp.dma_start(pre_tok[:, :], state_pool[0].rearrange("b t d -> (b t) d")).then_inc(s_pre, 16)
            for half in range(2):
                o = slice(half * HD, half * HD + HD)
                sp.dma_start(gains[o, 0:1], ins["g_q"][0].rearrange("(d o) -> d o", o=1)).then_inc(s_par, 16)
                sp.dma_start(gains[o, 1:2], ins["g_k"].rearrange("(d o) -> d o", o=1)).then_inc(s_par, 16)
            sp.dma_start(bias_f[:, :], ins["b_f"].rearrange("(d o) -> d o", o=1)).then_inc(s_par, 16)
            sp.dma_start(wf_sb[:, :, :], ins["w_f"].rearrange("(k p) h -> p k h", p=P)).then_inc(s_par, 16)
            sp.dma_start(pt_sb[:, :], page_table.rearrange("(o b) n -> o (b n)", o=1)).then_inc(s_par, 16)
            sp.dma_start(st_s[0][:, 0:BUF - TS, :], state_pool[0][:, TS:BUF, :]).then_inc(out_dma, 16)
            weights_in(sp)
            for s_, v_ in ((out_dma, 16), (st_out, 32), (proj_k.sent, 32 * KT), (proj_v.sent, 32 * KT), (lf_out, 32),
                           (y_out[0], 16 * ((NTT + 1) // 2)), (y_out[1], 16 * (NTT // 2))):
                sp.wait_ge(s_, v_)

        @block.gpsimd
        def _(pool):
            pool.memset(ident[:, :], 0.0).then_inc(const_ready, 1)
            pool.memset(ones[:, :], 1.0).then_inc(const_ready, 1)
            pool.memset(eps_c[:, :], EPS).then_inc(const_ready, 1)
            pool.memset(block_ones[:, :], 0.0).then_inc(const_ready, 1)
            pool.memset(ext[:, :, 0:BUF], 0.0).then_inc(const_ready, 1)
            pool.iota(cnt_i[:, :], pattern=[[1, 16]], base=1, channel_multiplier=0).then_inc(const_ready, 1)
            pool.wait_ge(const_ready, 6)
            pool.memset(block_ones[0:HD, 0:HD], 1.0).then_inc(const_ready, 1)
            pool.wait_ge(const_ready, 7)
            pool.memset(block_ones[HD:P, HD:P], 1.0).then_inc(const_ready, 1)
            pool.wait_ge(const_ready, 8)
            pool.affine_select(out=ident[:, :], in_=ident[:, :], compare_op=ALU.not_equal, fill=1.0, base=0,
                               pattern=[[-1, P]], channel_multiplier=1).then_inc(const_ready, 1)
            split_weights(pool, 0, n_of["mlp0"])
            split_weights(pool, n_of["mlp0"], 2)
            norm_mlp[0].pool(pool)
            split_weights(pool, n_of["mlp0"] + 2, n_mlp - 2)
            split_weights(pool, n_of["q"], 2)
            norm_q.pool(pool)
            split_weights(pool, n_of["q"] + 2, KT - 2)
            norm_kv.pool(pool)
            keep = proj_k.pool(pool)
            def k_block(i, j, n, k16, m):
                pool.wait_ge(w_in[j], k16)
                pool.wait_ge(w_used, n - 1)
                apart(pool)
                pool.tensor_copy(w_hi[:, j, :], w_raw[:, j, :]).then_inc(w_split, 1)
                pool.wait_ge(w_split, n * 2 + 1)
                pool.tensor_tensor(w_lo[:, j, :], w_raw[:, j, :], w_hi[:, j, :].bitcast(F32),
                                   ALU.subtract).then_inc(w_split, 1)
                if m is not None:
                    keep(m)
            n0 = n_of["k"]
            for j in range(2):
                k_block(0, j, n0 + j, 16 * ((n0 + j) // 2 + 1) + 16, None)
            pool.wait_ge(f_dve, 5)
            with pool.Fori(1, KT // 2, 1) as i:
                for j in range(2):
                    k_block(i, j, i * 2 + (n0 + j), i * 16 + (16 * (n0 // 2) + 32), i * 2 + (j - 2))
            keep(KT - 2)
            keep(KT - 1)
            split_weights(pool, n_of["v"], KT)
            sample_pool(pool)
            prompt_pool(pool)
            split_weights(pool, n_of["o"], KT)
            split_weights(pool, n_of["mlp1"], 2)
            norm_mlp[1].pool(pool)
            split_weights(pool, n_of["mlp1"] + 2, n_mlp - 2)

        @block.tensor
        def _(pe):
            pe.wait_ge(const_ready, 9)
            for t in range(NTT):
                w = P if t < NQ else S
                pe.wait_ge(s_x[t % 2], 16 * (t // 2 + 1))
                for b in range(2):
                    n = 2 * t + b
                    if n >= 4:
                        pe.wait_ge(x_cp, n - 3)
                    for k in range(4):
                        last = pe.transpose(ps[:, n % 4, k * P:k * P + w],
                                            x_tok[0:w, t % 2, (4 * b + k) * P:(4 * b + k + 1) * P], ident[0:w, 0:w])
                    last.then_inc(x_tr, 1)
                if t == 1:
                    pe.wait_ge(s_vec, 96)
                    pe.transpose(ps[:, 4, 0:6 * KT], vec_rows[:, :], ident[0:6 * KT, 0:6 * KT]).then_inc(vec_tr, 1)
                    pe.wait_ge(s_pre, 16)
                    for b in range(2):
                        for k in range(4):
                            last = pe.transpose(ps[:, 5 + b, k * P:k * P + NB * BUF],
                                                pre_tok[:, (4 * b + k) * P:(4 * b + k + 1) * P],
                                                ident[0:NB * BUF, 0:NB * BUF])
                        last.then_inc(pre_tr, 1)
            pe.wait_ge(x_cp, 2 * NTT)
            norm_pool.pe(pe)
            pe.wait_ge(st_cp, 1)
            pe.wait_ge(zeroed, KT)
            for b in range(2):
                for k in range(4):
                    last = pe.transpose(ps[0:BUF + S, 6 + b, k * P:(k + 1) * P], st_cols[:, 4 * b + k, :], ident[:, :])
                last.then_inc(st_tr, 1)
            for half in range(2):
                pe.wait_ge(w_split, 2 * half + 2)
                for gg in range(2):
                    g = 2 * half + gg
                    pe.wait_ge(pool_lo, g + 1)
                    for dt in range(2):
                        m = 2 * g + dt
                        for c in range(NC):
                            if m >= 2:
                                pe.wait_ge(mixed, 3 * (m - 2) + c + 1)
                            last = products(pe, half, 0, 2, c, NC * (m % 2) + c,
                                            lambda k, c: xn_hi[:, 2 * g + k, chunk(c)],
                                            lambda k, c: xn_lo[:, 2 * g + k, chunk(c)],
                                            stride=2 * P, off=512 * gg + P * dt)
                            last.then_inc(mix_full, 1)
                pe.drain().then_inc(w_used, 1)
            norm_mlp[0].pe(pe)
            mlps[0].pe(pe)
            norm_q.pe(pe)
            proj_q.pe(pe)
            pe.wait_ge(norm_kv.xn, KT * NC)
            pe.wait_ge(proj_q.copied, 3 * KT)
            for c in range(NC):
                for k in range(KT):
                    last = pe.matmul(ps[0:NH, c, 0:CH], wf_sb[:, k, :], norm_kv.tmp[:, c, k, :], start=(k == 0),
                                     stop=(k == KT - 1))
                last.then_inc(f_full, 1)
            pe.wait_ge(f_act, 3)
            proj_k.pe(pe)
            pe.wait_ge(proj_k.copied, 3 * KT)
            proj_v.pe(pe)
            pe.wait_ge(f_dve, 5)
            pe.wait_ge(proj_v.ev, 3 * KT)
            for t in range(NTT):
                w = min(P, N - t * P)
                last = pe.transpose(ps[0:w, 7, t * NH:(t + 1) * NH], lf_row[:, t * P:t * P + w], ident[0:NH, 0:NH])
            last.then_inc(f_tr, 1)
            sample_pe(pe)
            pe.wait_ge(a_ev, 2 * NB)
            pe.wait_ge(a_const, 4)
            prompt_pe(pe)
            proj_o.pe(pe)
            norm_mlp[1].pe(pe)
            mlps[1].pe(pe)
            pe.wait_ge(mlps[1].added, 3 * KT * NG)
            for t in range(NTT):
                w = min(P, N - t * P)
                for b in range(2):
                    n = 2 * t + b
                    if n >= 4:
                        pe.wait_ge(y_cp, n - 3)
                    for k in range(4):
                        last = pe.transpose(ps[0:w, n % 4, k * P:(k + 1) * P], h[:, 4 * b + k, t * P:t * P + w],
                                            ident[:, :])
                    last.then_inc(y_tr, 1)

        @block.scalar
        def _(act):
            norm_pool_squares(act)
            for g in range(4):
                act.wait_ge(pooled, g + 1)
                act.activation(xn_hi[:, 2 * g:2 * g + 2, :], win[g % 2][:, :, 0:N], ACT.Copy).then_inc(pool_hi, 1)
            for b in range(2):
                act.wait_ge(st_tr, b + 1)
                act.activation(st_tok[:, b * 512:b * 512 + 512], ps[0:BUF + S, 6 + b, :], ACT.Copy).then_inc(st_cp, 1)
            act.wait_ge(st_cp, 3)
            act.dma_start(st_p[0, 0], st_tok[0:BUF, :]).then_inc(st_out, 16)
            act.dma_start(st_s[0][:, BUF - TS:BUF, :], st_tok[BUF:BUF + S, :]).then_inc(st_out, 16)
            norm_mlp[0].act(act)
            mlps[0].act(act)
            norm_q.act(act)
            proj_q.act(act)
            norm_kv.act(act)
            act.wait_ge(norm_kv.lo, NC)
            for c in range(NC):
                act.wait_ge(f_full, c + 1)
                act.activation(lf_z[:, chunk(c)], ps[0:NH, c, 0:CH], ACT.Identity, bias=bias_f[:, 0:1]).then_inc(f_act, 1)
            act.wait_ge(f_dve, 1)
            act.activation(lf_e[:, :], lf_a[:, :], ACT.Exp, scale=-1.0).then_inc(f_act, 1)
            act.wait_ge(f_dve, 2)
            act.activation(lf_l[:, :], lf_u[:, :], ACT.Ln).then_inc(f_act, 1)
            proj_k.act(act)
            proj_v.act(act)
            act.wait_ge(f_cp, 2)
            act.dma_start(lf_p[0].rearrange("(t p) h -> p t h", p=P), lfT[:, 0:NQ, :]).then_inc(lf_out, 16)
            act.dma_start(lf_s.rearrange("b t h -> (b t) h"), lfT[0:S, NQ, :]).then_inc(lf_out, 16)
            sample_act(act)
            prompt_act(act)
            act.wait_ge(o_ev, 4 * NP)
            for c in range(NC):
                act.activation(xn_hi[:, :, chunk(c)], qT[:, :, chunk(c)], ACT.Copy).then_inc(o_split_hi, 1)
            norm_mlp[1].act(act)
            mlps[1].act(act)
            for t in range(NTT):
                w = min(P, N - t * P)
                if t >= 2:
                    act.wait_ge(y_out[t % 2], 16 * (t // 2))
                for b in range(2):
                    act.wait_ge(y_tr, 2 * t + b + 1)
                    act.activation(y_tok[0:w, t % 2, b * 512:b * 512 + 512], ps[0:w, (2 * t + b) % 4, :],
                                   ACT.Copy).then_inc(y_cp, 1)
                act.wait_ge(y_cp, 2 * t + 2)
                dst = y_p[0, t * P:t * P + P, :] if t < NQ else y_s.rearrange("b t d -> (b t) d")
                act.dma_start(dst, y_tok[0:w, t % 2, :]).then_inc(y_out[t % 2], 16)

        @block.vector
        def _(dve):
            dve.wait_ge(s_par, 16 * 7)
            dve.tensor_scalar(gains[:, 2:3], gains[:, 0:1], 1.0 / HD ** 0.5, None, ALU.mult).then_inc(cnt_done, 1)
            dve.wait_ge(const_ready, 9)
            dve.tensor_copy(cnt_r[:, :], cnt_i[:, :]).then_inc(cnt_done, 1)
            dve.wait_ge(cnt_done, 2)
            dve.reciprocal(cnt_r[:, :], cnt_r[:, :]).then_inc(cnt_done, 1)
            dve.wait_ge(vec_cp, 1)
            dve.wait_ge(x_cp, 2 * NTT)
            dve.wait_ge(pre_cp, KT)

            def write_ext(c):
                c0, c1 = c * CH, (c + 1) * CH
                for k in range(KT):
                    gain = vecs[:, k:k + 1]
                    pe_ = min(c1, T)
                    dve.scalar_tensor_tensor(ext[:, k, BUF + c0:BUF + pe_], h[:, k, c0:pe_], gain,
                                             rms[:, c, 0:pe_ - c0], ALU.mult, ALU.mult).then_inc(ext_done, 1)
                    if c1 > T:
                        dst = ext[:, k, BUF + T:].rearrange("p (b e) -> p b e", e=EXT)[:, :, BUF:]
                        dve.scalar_tensor_tensor(dst, h[:, k, T:N].rearrange("p (b t) -> p b t", t=TS), gain,
                                                 rms[:, c, T - c0:CH].rearrange("p (b t) -> p b t", t=TS),
                                                 ALU.mult, ALU.mult).then_inc(ext_done, 1)
            norm_pool.dve(dve, write_ext)
            dve.wait_ge(ext_done, KT * 4)
            dve.tensor_copy(st_cols[:, :, 0:BUF], ext[:, :, T:T + BUF]).then_inc(st_cp, 0 + 1)
            for k in range(KT):
                dve.tensor_copy(st_cols[:, k, BUF:].rearrange("p (b t) -> p b t", t=TS),
                                ext[:, k, BUF + T:].rearrange("p (b e) -> p b e", e=EXT)[:, :, BUF:]).then_inc(zeroed, 1)
            n_win = 0
            for g, w in enumerate(WINDOWS):
                src = ext[:, 2 * g:2 * g + 2, :]
                steps = g + 1
                sh = 1
                for j in range(steps):
                    dst = win[(g + 1 + steps - 1 - j) % 2]
                    lo = 2 * sh - 1
                    dve.wait_ge(win_done, n_win)
                    if j == 0 and g:
                        dve.wait_ge(pool_lo, g)
                    dve.tensor_tensor(dst[:, :, lo:NE], src[:, :, lo:NE], src[:, :, lo - sh:NE - sh],
                                      ALU.add).then_inc(win_done, 1)
                    n_win += 1
                    src = dst
                    sh *= 2
                dve.wait_ge(win_done, n_win)
                dve.wait_ge(cnt_done, 3)
                for k in range(2):
                    dve.scalar_tensor_tensor(src[:, k, BUF:BUF + w - 1], src[:, k, BUF:BUF + w - 1], float(w),
                                             cnt_r[:, 0:w - 1], ALU.mult, ALU.mult).then_inc(win_done, 1)
                    n_win += 1
                dve.wait_ge(win_done, n_win)
                out = win[g % 2]
                for k in range(2):
                    e = ext[:, 2 * g + k, :]
                    dve.scalar_tensor_tensor(out[:, k, 0:T], src[:, k, BUF:BUF + T], 1.0 / w, e[:, BUF:BUF + T],
                                             ALU.mult, ALU.subtract).then_inc(win_done, 1)
                    new = lambda t: t[:, BUF + T:].rearrange("p (b e) -> p b e", e=EXT)[:, :, BUF:]
                    ins_ = dve.scalar_tensor_tensor(out[:, k, T:N].rearrange("p (b t) -> p b t", t=TS), new(src[:, k, :]),
                                                    1.0 / w, new(e), ALU.mult, ALU.subtract)
                    ins_.then_inc(win_done, 1)
                    n_win += 2
                dve.wait_ge(win_done, n_win)
                ins_ = dve.tensor_copy(out[:, 0, N:N + 1], out[:, 0, 0:1])
                ins_.then_inc(pooled, 1)
                dve.wait_ge(pool_hi, g + 1)
                dve.tensor_tensor(xn_lo[:, 2 * g:2 * g + 2, :], out[:, :, 0:N], xn_hi[:, 2 * g:2 * g + 2, :].bitcast(F32),
                                  ALU.subtract).then_inc(pool_lo, 1)
            for m in range(KT):
                for c in range(NC):
                    dve.wait_ge(mix_full, 3 * m + c + 1)
                    dve.scalar_tensor_tensor(h[:, m, chunk(c)], ps[:, NC * (m % 2) + c, 0:CH],
                                             vecs[:, KT + m:KT + m + 1], h[:, m, chunk(c)], ALU.mult,
                                             ALU.add).then_inc(mixed, 1)
            norm_mlp[0].dve(dve)
            mlps[0].dve(dve)
            norm_q.dve(dve)
            proj_q.dve(dve)
            norm_kv.dve(dve)
            dve.wait_ge(f_act, 3)
            dve.scalar_tensor_tensor(lf_a[:, :], lf_z[:, :], -1.0, lf_z[:, :], ALU.mult, ALU.max).then_inc(f_dve, 1)
            dve.wait_ge(f_act, 4)
            dve.tensor_scalar(lf_u[:, :], lf_e[:, :], 1.0, None, ALU.add).then_inc(f_dve, 1)
            dve.wait_ge(f_dve, 2)
            dve.scalar_tensor_tensor(lf_e[:, :], lf_u[:, :], -1.0, lf_e[:, :], ALU.add, ALU.subtract).then_inc(f_dve, 1)
            dve.wait_ge(f_act, 5)
            dve.wait_ge(f_dve, 3)
            dve.tensor_tensor(lf_l[:, :], lf_l[:, :], lf_e[:, :], ALU.subtract).then_inc(f_dve, 1)
            dve.wait_ge(f_dve, 4)
            dve.wait_ge(norm_kv.xn, KT * NC)
            dve.scalar_tensor_tensor(lf_row, lf_z[:, :], 0.0, lf_l[:, :], ALU.min, ALU.subtract).then_inc(f_dve, 1)
            proj_k.dve(dve)
            dve.wait_ge(f_tr, 1)
            dve.tensor_copy(lfT[:, 0:NQ, :], ps[:, 7, 0:NQ * NH].rearrange("p (t h) -> p t h", h=NH)).then_inc(f_cp, 1)
            dve.tensor_copy(lfT[0:S, NQ, :], ps[0:S, 7, NQ * NH:NTT * NH]).then_inc(f_cp, 1)
            dve.wait_ge(f_cp, 2)
            sample_dve(dve)
            prompt_dve(dve)
            for c in range(NC):
                dve.wait_ge(o_split_hi, c + 1)
                dve.tensor_tensor(xn_lo[:, :, chunk(c)], qT[:, :, chunk(c)], xn_hi[:, :, chunk(c)].bitcast(F32),
                                  ALU.subtract).then_inc(o_split_lo, 1)

            def add_o(m, par, first):
                for c in range(NC):
                    dve.wait_ge(proj_o.full, m * 3 + (c + 1))
                    hm = h[:, bass.ds(m, 1), chunk(c)].rearrange("p o t -> p (o t)")
                    dve.tensor_tensor(hm, ps[:, NC * par + c, 0:CH], hm, ALU.add).then_inc(o_added, 1)
            proj_o.tiles(dve, add_o)
            norm_mlp[1].dve(dve)
            mlps[1].dve(dve)


_INS = ["x_prompt", "x_sample", "state_pool", "cache_k", "cache_v", "cache_logf", "page_table", "g_pool", "w_pool",
        "pool_scale", "g_attn", "w_q", "g_q", "w_o", "g_kv", "w_k", "w_v", "g_k", "w_f", "b_f", "g_mlp", "w_up", "w_down"]


def kernel(**inputs):
    import numpy as _np
    import concourse.bacc as _bacc
    from concourse import mybir as _mybir
    from concourse.bass_utils import run_bass_kernel_spmd as _run

    nc = _bacc.Bacc("TRN2", target_bir_lowering=False, num_devices=1, dynamic_dma_scratch_size=8192)
    arrays, ins = {}, {}
    for name in _INS:
        a = _np.ascontiguousarray(inputs[name])
        arrays[f"in_{name}"] = a
        ins[name] = nc.dram_tensor(f"in_{name}", a.shape, _mybir.dt.from_np(a.dtype), kind="ExternalInput").ap()
    b, t, d = inputs["x_prompt"].shape
    sb, ts, _ = inputs["x_sample"].shape
    la, _, buf, _ = inputs["state_pool"].shape
    _, _, nh, hd = inputs["cache_k"].shape
    shapes = [(b, t, d), (sb, ts, d), (la, b, buf, d), (la, sb, buf, d), (b, t, nh, hd), (b, t, nh, hd), (b, t, nh),
              (sb, ts, nh, hd), (sb, ts, nh, hd), (sb, ts, nh)]
    outs = [nc.dram_tensor(f"out_{i}", s, _mybir.dt.float32, kind="ExternalOutput").ap() for i, s in enumerate(shapes)]
    decoder_step(nc, ins, outs)
    r = _run(nc, [arrays], core_ids=[0])
    return tuple(r.results[0][f"out_{i}"] for i in range(len(outs)))
```
